# Optimizing a Trainium2 kernel written in Bass

```python
import math
import jax, jax.numpy as jnp
from jax import lax
import numpy as np

D_MODEL = 1024
BATCH = 1
SEQ = 1024
DEPTH = 1

CHUNK = 64
Q_BLOCK = 128

CONV_WIDTH = 512
CONV_GROUPS = 8
CONV_K = 3

MLA_HEADS = 4
QK_NOPE = 128
QK_ROPE = 64
QK_HEAD = QK_NOPE + QK_ROPE
V_HEAD = 128
Q_LORA = 384
KV_LORA = 256
MLA_WIDTH = MLA_HEADS * V_HEAD
ROPE_THETA = 10000.0

MIX_WIDTH = CONV_WIDTH + MLA_WIDTH
IN_PROJ = 3 * CONV_WIDTH + Q_LORA + KV_LORA + QK_ROPE

N_EXPERTS = 32
TOP_K = 4
D_FF = 1024
SWIGLU_LIMIT = 7.0
SWIGLU_ALPHA = 1.702

EPS = 1e-6

kernel_name = "hymba_conv_mla_moe_streaming_block"

def rmsnorm(x, g):
    xf = x.astype(jnp.float32)
    y = xf * lax.rsqrt(jnp.mean(xf * xf, axis=-1, keepdims=True) + EPS)
    return (y * g.astype(jnp.float32)).astype(x.dtype)

def rope(x, pos):
    half = QK_ROPE // 2
    inv_freq = ROPE_THETA ** (-jnp.arange(half, dtype=jnp.float32) / half)
    ang = pos.astype(jnp.float32)[:, None] * inv_freq[None, :]
    cos = jnp.cos(ang)[None, :, None, :].astype(x.dtype)
    sin = jnp.sin(ang)[None, :, None, :].astype(x.dtype)
    x1, x2 = x[..., :half], x[..., half:]
    return jnp.concatenate([x1 * cos - x2 * sin, x1 * sin + x2 * cos], axis=-1)

def short_conv_mixer(b_gate, c_gate, x_in, conv_w):
    u = c_gate * x_in
    y = lax.conv_general_dilated(
        u, conv_w[:, None, :],
        window_strides=(1,), padding=[(CONV_K - 1, 0)],
        dimension_numbers=("NWC", "WIO", "NWC"),
        feature_group_count=CONV_WIDTH)
    return b_gate * y

def mla_mixer(c_q, c_kv, k_pe, q_norm, w_uq, kv_norm, w_ukv, q_head_norm, k_head_norm):
    bsz, seq = c_q.shape[0], c_q.shape[1]
    pos = jnp.arange(seq)
    q = (rmsnorm(c_q, q_norm) @ w_uq).reshape(bsz, seq, MLA_HEADS, QK_HEAD)
    kv = (rmsnorm(c_kv, kv_norm) @ w_ukv).reshape(bsz, seq, MLA_HEADS, QK_NOPE + V_HEAD)
    k_nope, v = kv[..., :QK_NOPE], kv[..., QK_NOPE:]
    k_pe_h = jnp.broadcast_to(k_pe[:, :, None, :], (bsz, seq, MLA_HEADS, QK_ROPE))
    k = jnp.concatenate([k_nope, k_pe_h], axis=-1)
    q = rmsnorm(q, q_head_norm)
    k = rmsnorm(k, k_head_norm)
    q = jnp.concatenate([q[..., :QK_NOPE], rope(q[..., QK_NOPE:], pos)], axis=-1)
    k = jnp.concatenate([k[..., :QK_NOPE], rope(k[..., QK_NOPE:], pos)], axis=-1)

    scale = 1.0 / math.sqrt(QK_HEAD)
    n_blk = seq // Q_BLOCK
    q_blocks = jnp.moveaxis(q.reshape(bsz, n_blk, Q_BLOCK, MLA_HEADS, QK_HEAD), 1, 0)
    k_chunk = jnp.arange(seq) // CHUNK
    neg = jnp.finfo(jnp.float32).min

    def attend(args):
        qb, i = args
        q_chunk = (i * Q_BLOCK + jnp.arange(Q_BLOCK)) // CHUNK
        allowed = k_chunk[None, :] <= q_chunk[:, None]
        s = jnp.einsum("bqhd,bkhd->bhqk", qb, k,
                       preferred_element_type=jnp.float32) * scale
        s = jnp.where(allowed[None, None], s, neg)
        p = jax.nn.softmax(s, axis=-1).astype(v.dtype)
        return jnp.einsum("bhqk,bkhd->bqhd", p, v)

    o = lax.map(attend, (q_blocks, jnp.arange(n_blk)))
    return jnp.moveaxis(o, 0, 1).reshape(bsz, seq, MLA_WIDTH)

def moe_ffn(h, w_router, b_router, w_gate_up, b_gate_up, w_down, b_down):
    bsz, seq, d = h.shape
    n_tok = bsz * seq
    hf = h.reshape(n_tok, d)
    logits = (hf @ w_router + b_router).astype(jnp.float32)
    top_vals, top_idx = lax.top_k(logits, TOP_K)
    gates = jax.nn.softmax(top_vals, axis=-1).astype(h.dtype)
    flat_e = top_idx.reshape(-1)
    order = jnp.argsort(flat_e)
    token_of = order // TOP_K
    e_sorted = flat_e[order]
    xs = hf[token_of]
    sizes = jnp.bincount(flat_e, length=N_EXPERTS).astype(jnp.int32)
    gu = lax.ragged_dot(xs, w_gate_up, sizes) + b_gate_up[e_sorted]
    gate = jnp.minimum(gu[:, :D_FF], SWIGLU_LIMIT)
    up = jnp.clip(gu[:, D_FF:], -SWIGLU_LIMIT, SWIGLU_LIMIT)
    act = (up + 1.0) * (gate * jax.nn.sigmoid(SWIGLU_ALPHA * gate))
    out = lax.ragged_dot(act, w_down, sizes) + b_down[e_sorted]
    out = out * gates.reshape(-1)[order][:, None]
    y = jax.ops.segment_sum(out, token_of, num_segments=n_tok)
    return y.reshape(bsz, seq, d)

def setup_inputs(seed: int = 0) -> dict:
    key = jax.random.key(seed)
    ks = jax.random.split(key, 18)

    def nrm(k, shape, scale):
        return jax.random.normal(k, shape, jnp.float32) * scale

    def gain(k, shape):
        return 1.0 + 0.02 * jax.random.normal(k, shape, jnp.float32)

    L = DEPTH
    return {
        "x": nrm(ks[0], (BATCH, SEQ, D_MODEL), 1.0),
        "norm_mix": gain(ks[1], (L, D_MODEL)),
        "w_in": nrm(ks[2], (L, D_MODEL, IN_PROJ), D_MODEL ** -0.5),
        "conv_w": nrm(ks[3], (L, CONV_K, CONV_WIDTH), CONV_K ** -0.5),
        "q_norm": gain(ks[4], (L, Q_LORA)),
        "w_uq": nrm(ks[5], (L, Q_LORA, MLA_HEADS * QK_HEAD), Q_LORA ** -0.5),
        "kv_norm": gain(ks[6], (L, KV_LORA)),
        "w_ukv": nrm(ks[7], (L, KV_LORA, MLA_HEADS * (QK_NOPE + V_HEAD)), KV_LORA ** -0.5),
        "q_head_norm": gain(ks[8], (L, QK_HEAD)),
        "k_head_norm": gain(ks[9], (L, QK_HEAD)),
        "w_o": nrm(ks[10], (L, MIX_WIDTH, D_MODEL), MIX_WIDTH ** -0.5),
        "norm_ffn": gain(ks[11], (L, D_MODEL)),
        "w_router": nrm(ks[12], (L, D_MODEL, N_EXPERTS), D_MODEL ** -0.5),
        "b_router": nrm(ks[13], (L, N_EXPERTS), 0.01),
        "w_gate_up": nrm(ks[14], (L, N_EXPERTS, D_MODEL, 2 * D_FF), D_MODEL ** -0.5),
        "b_gate_up": nrm(ks[15], (L, N_EXPERTS, 2 * D_FF), 0.02),
        "w_down": nrm(ks[16], (L, N_EXPERTS, D_FF, D_MODEL), D_FF ** -0.5),
        "b_down": nrm(ks[17], (L, N_EXPERTS, D_MODEL), 0.02),
    }

def reference(x, norm_mix, w_in, conv_w, q_norm, w_uq, kv_norm, w_ukv, q_head_norm,
              k_head_norm, w_o, norm_ffn, w_router, b_router, w_gate_up, b_gate_up,
              w_down, b_down):
    h = x
    splits = np.cumsum([CONV_WIDTH, CONV_WIDTH, CONV_WIDTH, Q_LORA, KV_LORA]).tolist()
    for l in range(DEPTH):
        hn = rmsnorm(h, norm_mix[l])
        proj = hn @ w_in[l]
        b_gate, c_gate, x_in, c_q, c_kv, k_pe = jnp.split(proj, splits, axis=-1)
        conv_out = short_conv_mixer(b_gate, c_gate, x_in, conv_w[l])
        attn_out = mla_mixer(c_q, c_kv, k_pe, q_norm[l], w_uq[l], kv_norm[l],
                             w_ukv[l], q_head_norm[l], k_head_norm[l])
        h = h + jnp.concatenate([conv_out, attn_out], axis=-1) @ w_o[l]
        h = h + moe_ffn(rmsnorm(h, norm_ffn[l]), w_router[l], b_router[l],
                        w_gate_up[l], b_gate_up[l], w_down[l], b_down[l])
    return h


_drawn_inputs = setup_inputs


def setup_inputs(seed=0):
    import zlib

    import numpy as np

    out = dict(_drawn_inputs(seed))
    spreads = {}
    factors = {'q_norm': 5.887,
     'kv_norm': 4.949,
     'q_head_norm': 7.746,
     'k_head_norm': 8.0,
     'b_gate_up': 16.595,
     'b_down': 19.199,
     'norm_ffn': 4.252,
     'b_router': 5.422}
    for name, (base, spread) in spreads.items():
        noise = np.random.default_rng([zlib.crc32(name.encode()), seed]).standard_normal(out[name].shape)
        drawn = base * np.exp(spread * noise) if base else spread * noise
        out[name] = __import__('jax').numpy.asarray(drawn.astype(out[name].dtype))
    for name, factor in factors.items():
        out[name] = (out[name] * factor).astype(out[name].dtype)
    return out
```

```python
from contextlib import ExitStack, contextmanager

import numpy as np

import concourse.bass as bass
from concourse import mybir

ALU = mybir.AluOpType
ACT = mybir.ActivationFunctionType
AX_X = mybir.AxisListType.X
F32 = mybir.dt.float32
BF16 = mybir.dt.bfloat16
I32 = mybir.dt.int32
U32 = mybir.dt.uint32

P = 128
SEQ, D = 1024, 1024
NT = SEQ // P
KD = D // P
CONV, TAPS = 512, 3
NF = CONV // P
HEADS, NOPE, ROPE, VH = 4, 128, 64, 128
HALF = ROPE // 2
QKH = NOPE + ROPE
QL, KVL = 384, 256
LOW = QL + KVL + ROPE
IN_PROJ = 3 * CONV + LOW
QW, KVW = HEADS * QKH, HEADS * (NOPE + VH)
NCQ, NCKV = QL // P, KVL // P
E, TOPK, FF = 32, 4, 1024
LIMIT, ALPHA = 7.0, 1.702
EPS = 1e-6
THETA = 10000.0
CHUNK = 64
SCALE = 1.0 / QKH ** 0.5
NEG = -3.0e38

SLOTS = 160
SLOTS_B = SLOTS - P
MAX_TILES = E + (SEQ * TOPK - E) // SLOTS
LEVELS = -(-SEQ // SLOTS)
GROUP = 6
GROUPS = -(-(MAX_TILES + 1) // GROUP)
TABLE = 68
WIDTHS = [P, 132, 136, 141, 146, 152, SLOTS]
PIECES = 12
PIECE = 2048
NC = FF // P
ROUTE = 6


def constants():
    tok = np.arange(SEQ, dtype=np.float32).reshape(NT, P)
    inv = (np.float32(THETA) ** (-np.arange(HALF, dtype=np.float32) / np.float32(HALF))).astype(np.float32)
    ang = (tok[:, :, None] * inv[None, None, :]).astype(np.float32)
    cos = np.cos(ang).astype(np.float32).transpose(1, 0, 2).reshape(P, NT * HALF)
    sin = np.sin(ang).astype(np.float32).transpose(1, 0, 2).reshape(P, NT * HALF)
    p = np.arange(P, dtype=np.float32)[:, None]
    parts = {
        "ident": np.eye(P, dtype=np.float32),
        "before": (p < np.arange(P, dtype=np.float32)[None, :]).astype(np.float32),
        "ones": np.ones((P, P), np.float32),
        "slot": np.tile(np.arange(SLOTS, dtype=np.float32), (P, 1)),
        "cos": cos, "sin": sin, "nsin": -sin,
        "expert": np.tile(np.arange(E, dtype=np.float32), (P, 1)),
        "pad": np.concatenate([SEQ + p, SEQ + P + p], 1),
        "npad": np.concatenate([-(SEQ + p), -(SEQ + P + p)], 1),
        "tokp": p,
        "tilebase": np.tile(np.arange(NT, dtype=np.float32) * P, (P, 1)),
        "eps": np.full((P, 1), EPS, np.float32),
    }
    at, where = 0, {}
    for name, a in parts.items():
        where[name] = (at, a.shape[1])
        at += a.shape[1]
    return np.ascontiguousarray(np.concatenate(list(parts.values()), 1).astype(np.float32)), where


def attention_steps():
    steps = []
    units = NT * HEADS
    for n in range(units + 2):
        i, h = n // HEADS, n % HEADS
        if n < units:
            steps.append(("S", n))
        if n >= 2:
            steps.append(("PV", n - 2))
        if h == 0 and i > 1:
            steps.append(("WO", 2 * (i - 2) + 1))
        if h == 2 and i > 1:
            steps.append(("HT", i - 2))
        if h == 2 and i:
            steps.append(("OT", i - 1))
        if h == 3 and i > 1:
            steps.append(("RT", i - 2))
        if h == 3 and i:
            steps.append(("WO", 2 * (i - 1)))
        if 0 < n <= units:
            steps.append(("TP", n - 1))
    e = NT - 1
    return steps + [("OT", e), ("HT", e - 1), ("RT", e - 1), ("WO", 2 * e), ("WO", 2 * e + 1), ("HT", e), ("RT", e)]


def tiles(eng, body):
    body(0, True, False)
    with eng.Fori(1, NT - 1) as i:
        body(i, False, False)
    body(NT - 1, False, True)


@contextmanager
def expert_tiles(eng, used):
    with eng.Fori(0, GROUPS * GROUP, GROUP) as first:
        with eng.If(first < used):
            with eng.Fori(first, first + GROUP) as t:
                yield t


class Chain:

    def __init__(self, eng, sem, wait=None):
        self.wait, self.sem, self.base, self.n = wait or eng.wait_ge, sem, 0, 0

    def at(self, base):
        self.base, self.n = base, 0

    def link(self, ins):
        self.n += 1
        ins.then_inc(self.sem, 1)
        self.wait(self.sem, self.base + self.n)


def mid(ap, n):
    return ap.rearrange("p (o n) -> p o n", o=1).to_broadcast([ap.shape[0], n, ap.shape[1]])


def last(ap, n):
    return ap.rearrange("p (n o) -> p n o", o=1).to_broadcast([ap.shape[0], ap.shape[1], n])


def build(nc, I, out):
    consts_np, where = constants()
    NCONST = consts_np.shape[1]
    consts_dram = nc.inline_tensor(consts_np, name="shape_constants").ap()
    ctx = ExitStack()
    with ctx:
        def sb(name, shape, dt=F32):
            return ctx.enter_context(nc.sbuf_tensor(name, shape, dt))

        def sem(name):
            return ctx.enter_context(nc.semaphore(name))

        consts = sb("consts", [P, NCONST])
        K = {n: consts[:, a:a + w] for n, (a, w) in where.items()}
        ident, ones = K["ident"], K["ones"]
        cosT = K["cos"].rearrange("p (t n) -> p t n", t=NT)
        sinT = K["sin"].rearrange("p (t n) -> p t n", t=NT)
        nsinT = K["nsin"].rearrange("p (t n) -> p t n", t=NT)
        g_mix = sb("g_mix", [P, KD])
        g_q = sb("g_q", [P, NCQ + NCKV])
        taps = sb("taps", [P, TAPS, NF])
        gq_row = sb("gq_row", [P, QKH])
        gk_row = sb("gk_row", [P, QKH])
        stat = sb("stat", [P, 40])
        attn_stat = sb("attn_stat", [P, 128])
        gsum = sb("gsum", [P, 2])
        psum = ctx.enter_context(nc.psum_tensor("psum", [P, 8 * 512], F32))
        bank = [psum[:, b * 512:(b + 1) * 512] for b in range(8)]

        AREA = 51190
        area = sb("area", [P, AREA])

        def view(off, *dims):
            n = int(np.prod(dims))
            assert off + n <= AREA, (off, n)
            v = area[:, off:off + n]
            if len(dims) == 2:
                return v.rearrange("p (a b) -> p a b", a=dims[0])
            if len(dims) == 3:
                return v.rearrange("p (a b c) -> p a b c", a=dims[0], b=dims[1])
            return v

        o = 0

        def take(*dims):
            nonlocal o
            v = view(o, *dims)
            o += int(np.prod(dims))
            return v

        w_in = take(KD, IN_PROJ)
        w_uq = take(NCQ, QW)
        w_ukv = take(NCKV, KVW)
        xt, hn, hnT = take(D), take(D), take(KD, P)
        WIDE_END = o
        cn = take(LOW)
        cT = take(NCQ + NCKV, P)
        q_raw, q_rot = take(HEADS, QKH), take(HEADS * ROPE)
        k_nope, k_rot = take(HEADS, NOPE), take(HEADS * ROPE)
        kp_rot = take(ROPE)
        u = take(NF, P + TAPS - 1)
        conv_y, conv_t = take(NF, P), take(NF, P)
        rope_t = take(2 * HEADS * ROPE)
        kp_t = rope_t[:, 0:2 * ROPE]
        c_gate = conv_t
        SMALL_END = o
        convT = take(NF, SEQ)
        KEEP = o
        qT_n, kT_n = take(HEADS, SEQ), take(HEADS, SEQ)
        qT_r, kT_r = take(HEADS // 2, SEQ), take(HEADS // 2, SEQ)
        v_sb = take(NT, HEADS * VH)
        ALL_END = o

        o = 0
        w_o = take(KD, D)
        prob = [take(SEQ) for _ in range(2)]
        probT = [take(NT, P) for _ in range(2)]
        o_sb, attnT = take(HEADS * VH), take(HEADS, P)
        h_sb = [take(D) for _ in range(2)]
        hf, hfT = take(D), take(KD, P)
        gf_row = take(D)
        w_r = take(KD, E)
        mask, gate = take(NT, E), take(NT, E)
        RING_LOW = o
        LOW_SLOTS = (WIDE_END - RING_LOW) // PIECE
        slot_at = [RING_LOW + s * PIECE for s in range(LOW_SLOTS)]
        slot_at += [SMALL_END + s * PIECE for s in range(PIECES - LOW_SLOTS)]
        assert slot_at[-1] + PIECE <= ALL_END
        slots = [view(a, PIECE) for a in slot_at]
        w_gu = [slots[s].rearrange("p (k n) -> p k n", k=KD) for s in range(8)]
        w_dn = [slots[8 + s].rearrange("p (k n) -> p k n", k=2) for s in range(4)]
        o = WIDE_END
        bguT, bdT = take(2 * NC, E), take(KD, E)
        bias_rows = take(2 * FF + D)
        lg, top8, idx8, idxf, em, br_row = take(E), take(8), take(8), take(8), take(E), take(E)
        idx8 = idx8.bitcast(U32)
        assert o <= SMALL_END

        o = 0
        xg_a, xg_b = take(D), take(D)
        xT, actT, outT = take(KD, SLOTS), take(NC, SLOTS), take(KD, SLOTS)
        rows_a, rows_b = take(D), take(D)
        g_c, u_c, sg, gs_t = take(2, SLOTS), take(2, SLOTS), take(2, SLOTS), take(SLOTS)
        u2_t = take(SLOTS)
        sel = take(NT, SLOTS // 2).rearrange("p t n -> p (t n)").bitcast(BF16).rearrange("p (t n) -> p t n", t=NT)
        route = take(NT * E * ROUTE // 2).bitcast(BF16).rearrange("p (t e c) -> p t e c", t=NT, e=E)
        rank = take(NT, E)
        off = take(NT + 1, E)
        rl = take(NT)
        cum = take(2, E)
        used = take(E)
        first_t, past_e, at_e, prod = take(E), take(E), take(E), take(2, E)
        tab, spread = take(3), take(P)
        jt_f = take(TABLE)
        held_i = take(TABLE).bitcast(I32)
        te_i, n_i = take(TABLE).bitcast(I32), take(1).bitcast(I32)
        row_a, row_b = take(TABLE).bitcast(U32), take(TABLE).bitcast(U32)
        gate_a, gate_b = take(TABLE), take(TABLE)
        pick_a, pick_b, put_a, put_b = (take(1).bitcast(U32) for _ in range(4))
        ix_a, ix_b = take(ROUTE + 2), take(ROUTE + 2)
        res_t, part = take(NT, E), take(NT, E)
        assert o <= RING_LOW - 2 * NT * E, o

        hf_dram = nc.dram_tensor("normed_rows", (SEQ + SLOTS, D), F32, kind="Internal").ap()
        acc_dram = nc.dram_tensor("sum_rows", (SEQ + SLOTS, D), F32, kind="Internal").ap()

        x_rows = I["x"][0].rearrange("(t p) n -> t p n", p=P)
        w_in_v = I["w_in"][0].rearrange("(k p) n -> p k n", p=P)
        w_gu_v = I["w_gate_up"][0].rearrange("e (k p) n -> e p k n", p=P)
        w_dn_v = I["w_down"][0].rearrange("e (k p) n -> e p k n", p=P)

        consts_in, g_mix_in, small_in, x_in = sem("consts_in"), sem("g_mix_in"), sem("small_in"), sem("x_in")
        w_low_in, w_cx_in, w_b_in, w_uq_in, w_ukv_in = (sem(n) for n in ("w_low_in", "w_cx_in", "w_b_in", "w_uq_in", "w_ukv_in"))
        x_sq, x_std, x_rstd, hn_ready = sem("x_sq"), sem("x_std"), sem("x_rstd"), sem("hn_ready")
        hn_turned, hnT_ready = sem("hn_turned"), sem("hnT_ready")
        low_done, c_sq, c_std, c_rstd, c_ready = sem("low_done"), sem("c_sq"), sem("c_std"), sem("c_rstd"), sem("c_ready")
        c_turned, cT_ready = sem("c_turned"), sem("cT_ready")
        cx_done, u_ready, y_ready, b_done, conv_done = sem("cx_done"), sem("u_ready"), sem("y_ready"), sem("b_done"), sem("conv_done")
        q_proj, kv_proj, head_sq, v_ready = sem("q_proj"), sem("kv_proj"), sem("head_sq"), sem("v_ready")
        head_sum, head_std, head_rstd = sem("head_sum"), sem("head_std"), sem("head_rstd")
        q_normed, k_normed, k_rot_ready, q_rot_ready, kp_ready = (sem(n) for n in ("q_normed", "k_normed", "k_rot_ready", "q_rot_ready", "kp_ready"))
        qk_turned, qT_ready, kT_ready = sem("qk_turned"), sem("qT_ready"), sem("kT_ready")
        pool_chain, dve_chain = sem("pool_chain"), sem("dve_chain")
        w_o_in, w_r_in, row_in, bias_in = sem("w_o_in"), sem("w_r_in"), sem("row_in"), sem("bias_in")
        bias_turned, bias_ready = sem("bias_turned"), sem("bias_ready")
        s_done, s_max, exp_done = sem("s_done"), sem("s_max"), sem("exp_done")
        turn_a, turn_a_read, turn_b, turn_b_read = sem("turn_a"), sem("turn_a_read"), sem("turn_b"), sem("turn_b_read")
        pv_done, o_ready, wo_done, h_ready = sem("pv_done"), sem("o_ready"), sem("wo_done"), sem("h_ready")
        hx_in = [sem(f"hx_in{b}") for b in range(2)]
        h_sq, h_std, h_rstd, hf_ready = sem("h_sq"), sem("h_std"), sem("h_rstd"), sem("hf_ready")
        h_out, hf_out = sem("h_out"), sem("hf_out")
        rt_done, lg_read, top_ready, e_ready, gate_ready = (sem(n) for n in ("rt_done", "lg_read", "top_ready", "e_ready", "gate_ready"))
        zero_ready, zero_out = sem("zero_ready"), sem("zero_out")
        pool_passed = sem("pool_passed")
        pick_ready, put_ready = sem("pick_ready"), sem("put_ready")
        rank_mm, tables_ready, route_ready = sem("rank_mm"), sem("tables_ready"), sem("route_ready")
        tab_ready, tab_turned = sem("tab_ready"), sem("tab_turned")
        w_exp_in = [sem(f"w_exp_in{s}") for s in range(PIECES)]
        early_in = sem("early_in")
        sel_ready, idx_done, idx_ready, gathered = sem("sel_ready"), sem("idx_done"), sem("idx_ready"), sem("gathered")
        x_turned, xT_ready = sem("x_turned"), sem("xT_ready")
        gu_done, gu_read, sig_ready, act_ready = sem("gu_done"), sem("gu_read"), sem("sig_ready"), sem("act_ready")
        down_done, outT_ready = sem("down_done"), sem("outT_ready")
        rows_turned, rows_ready, rows_free, scattered, final_out = (sem(n) for n in ("rows_turned", "rows_ready", "rows_free", "scattered", "final_out"))

        block = ctx.enter_context(nc.Block())
        steps = attention_steps()
        use_a, use_b = {}, {}
        for st in steps:
            kind, n = st
            if kind in ("TP", "OT", "HT"):
                use_a[st] = len(use_a) + 1
            if kind == "HT" or (kind == "TP" and n // HEADS >= 4):
                use_b[st] = len(use_b) + 1

        RT_H, halves = {}, 0
        for kind, n in steps:
            halves += kind == "WO"
            if kind == "RT":
                RT_H[n] = halves

        @block.sync
        def _(sp):
            sp.dma_start(xt, x_rows[0]).then_inc(x_in, 16)
            sp.dma_start(consts[:], consts_dram).then_inc(consts_in, 16)
            sp.dma_start(g_mix[:], I["norm_mix"][0].rearrange("(k p) -> p k", p=P), allow_slow_non_contiguous=True).then_inc(g_mix_in, 16)
            sp.dma_start(w_in[:, :, 3 * CONV:], w_in_v[:, :, 3 * CONV:]).then_inc(w_low_in, 16)
            sp.dma_start(g_q[:, 0:NCQ], I["q_norm"][0].rearrange("(k p) -> p k", p=P), allow_slow_non_contiguous=True).then_inc(small_in, 16)
            sp.dma_start(g_q[:, NCQ:], I["kv_norm"][0].rearrange("(k p) -> p k", p=P), allow_slow_non_contiguous=True).then_inc(small_in, 16)
            sp.dma_start(gq_row[:], I["q_head_norm"].to_broadcast([P, QKH])).then_inc(small_in, 16)
            sp.dma_start(gk_row[:], I["k_head_norm"].to_broadcast([P, QKH])).then_inc(small_in, 16)
            for j in range(TAPS):
                sp.dma_start(taps[:, j, :], I["conv_w"][0, j].rearrange("(k p) -> p k", p=P), allow_slow_non_contiguous=True).then_inc(small_in, 16)
            sp.dma_start(w_in[:, :, CONV:3 * CONV], w_in_v[:, :, CONV:3 * CONV]).then_inc(w_cx_in, 16)
            sp.dma_start(w_in[:, :, 0:CONV], w_in_v[:, :, 0:CONV]).then_inc(w_b_in, 16)
            sp.dma_start(w_uq, I["w_uq"][0].rearrange("(k p) n -> p k n", p=P)).then_inc(w_uq_in, 16)
            sp.dma_start(w_ukv, I["w_ukv"][0].rearrange("(k p) n -> p k n", p=P)).then_inc(w_ukv_in, 16)

            def load_x(i, first, last_tile):
                if last_tile:
                    return
                sp.wait_ge(hn_ready, i + 1)
                sp.dma_start(xt, x_rows[bass.ds(i + 1, 1)].rearrange("a p n -> (a p) n")).then_inc(x_in, 16)

            tiles(sp, load_x)

            sp.wait_ge(qk_turned, NT)
            sp.wait_ge(k_normed, HEADS * NT)
            sp.wait_ge(k_rot_ready, NT)
            sp.wait_ge(conv_done, NT)
            sp.wait_ge(q_rot_ready, NT)
            sp.wait_ge(y_ready, NT)
            sp.dma_start(bias_rows[0:E, 0:2 * FF], I["b_gate_up"][0]).then_inc(bias_in, 16)
            sp.dma_start(bias_rows[0:E, 2 * FF:], I["b_down"][0]).then_inc(bias_in, 16)
            sp.dma_start(br_row[0:1, :], I["b_router"]).then_inc(bias_in, 16)
            sp.dma_start(w_o, I["w_o"][0].rearrange("(k p) n -> p k n", p=P)).then_inc(w_o_in, 16)
            sp.dma_start(w_r, I["w_router"][0].rearrange("(k p) n -> p k n", p=P)).then_inc(w_r_in, 16)
            sp.dma_start(gf_row, I["norm_ffn"].to_broadcast([P, D])).then_inc(row_in, 16)
            for i in range(2):
                sp.dma_start(h_sb[i], x_rows[i]).then_inc(hx_in[i], 16)

            def weights(e, piece, signal):
                q = piece // 2
                if piece < 8:
                    col = q * 256 + (piece % 2) * FF
                    src = w_gu_v[bass.ds(e, 1), :, :, col:col + 256]
                    dst = w_gu[piece]
                else:
                    k = 2 * (piece - 8)
                    src = w_dn_v[bass.ds(e, 1), :, k:k + 2, :]
                    dst = w_dn[piece - 8]
                sp.dma_start(dst, src.rearrange("a p k n -> (a p) k n")).then_inc(signal, 16)

            for piece in range(LOW_SLOTS):
                weights(0, piece, early_in)
            for i in range(NT):
                b = i % 2
                sp.wait_ge(h_ready, 2 * (i + 1))
                sp.dma_start(acc_dram[i * P:(i + 1) * P, :], h_sb[b]).then_inc(h_out, 16)
                sp.wait_ge(hf_ready, i + 1)
                sp.dma_start(hf_dram[i * P:(i + 1) * P, :], hf).then_inc(hf_out, 16)
                if i + 2 < NT:
                    sp.wait_ge(h_out, 16 * (i + 1))
                    sp.dma_start(h_sb[b], x_rows[i + 2]).then_inc(hx_in[b], 16)
            sp.wait_ge(tables_ready, 1)
            n_tiles = sp.value_load(n_i[0:1, 0:1], min_val=1, max_val=MAX_TILES)
            e0 = sp.value_load(te_i[0:1, 0:1], min_val=0, max_val=E - 1)
            sp.wait_ge(early_in, 16 * LOW_SLOTS)
            with sp.If(e0 < 1):
                for piece in range(LOW_SLOTS):
                    sp.sem_inc(w_exp_in[piece], 16)
            with sp.Else():
                for piece in range(LOW_SLOTS):
                    weights(e0, piece, w_exp_in[piece])
            sp.wait_ge(gathered, 32)
            for piece in range(LOW_SLOTS, PIECES):
                weights(e0, piece, w_exp_in[piece])
            with sp.Fori(1, MAX_TILES) as t:
                with sp.If(t < n_tiles):
                    e = sp.value_load(te_i[0:1, bass.ds(t, 1)], min_val=0, max_val=E - 1)
                    for piece in range(PIECES):
                        if piece < 8 and piece % 2 == 0:
                            sp.wait_ge(gu_done, t * NC - NC + piece + 2)
                        if piece >= 8:
                            sp.wait_ge(down_done, t * 4 - 4 + piece - 7)
                        weights(e, piece, w_exp_in[piece])
            sp.wait_ge(rows_free, n_tiles + 2)
            sp.dma_start(out[0], acc_dram[0:SEQ, :]).then_inc(final_out, 16)
            sp.wait_ge(final_out, 16)

        @block.gpsimd
        def _(pool):
            g = nc.gpsimd

            def wait(sem, value):
                pool.wait_ge(sem, value)
                pool.sem_inc(pool_passed, 1)

            POOL_LINKS = 7
            ch = Chain(pool, pool_chain, wait)
            g.memset(u[:, :, 0:TAPS - 1], 0.0).then_inc(zero_ready, 1)

            def rotate(x, heads, i, dst, tmp):
                x4 = x.rearrange("p h (s n) -> p h s n", s=2)
                t4 = tmp.rearrange("p (c h s n) -> p c h s n", c=2, h=heads, s=2)
                cs, sn, ns = (a[:, bass.ds(i, 1), :].to_broadcast([P, heads, HALF]) for a in (cosT, sinT, nsinT))
                d4 = dst.rearrange("p (h s n) -> p h s n", h=heads, s=2)
                g.tensor_tensor(t4[:, 0, :, 0, :], x4[:, :, 0, :], cs, ALU.mult)
                g.tensor_tensor(t4[:, 0, :, 1, :], x4[:, :, 1, :], cs, ALU.mult)
                g.tensor_tensor(t4[:, 1, :, 0, :], x4[:, :, 1, :], ns, ALU.mult)
                ch.link(g.tensor_tensor(t4[:, 1, :, 1, :], x4[:, :, 0, :], sn, ALU.mult))
                return g.tensor_tensor(dst, tmp[:, 0:heads * ROPE], tmp[:, heads * ROPE:2 * heads * ROPE], ALU.add)

            zeros = v_sb[:, 0:2, :].rearrange("p a n -> p (a n)")
            g.memset(zeros, 0.0).then_inc(zero_ready, 1)
            wait(zero_ready, 2)
            for dram in (hf_dram, acc_dram):
                pool.dma_start(dram[SEQ:SEQ + P, :], zeros).then_inc(zero_out, 16)
                pool.dma_start(dram[SEQ + P:, :], zeros[0:SLOTS_B, :]).then_inc(zero_out, 16)
            wait(consts_in, 16)
            wait(small_in, 16 * 7)

            def body(i, first, last_tile):
                ch.at(i * POOL_LINKS)
                wait(c_ready, i * 3 + 3)
                if not first:
                    wait(k_rot_ready, i)
                    wait(q_rot_ready, i)
                kp3 = cn[:, QL + KVL:LOW].rearrange("p (h n) -> p h n", h=1)
                rotate(kp3, 1, i, kp_rot, kp_t).then_inc(kp_ready, 1)
                wait(u_ready, i + 1)
                if not first:
                    wait(conv_done, i)
                ch.link(g.tensor_tensor(conv_y, u[:, :, 0:P], last(taps[:, 0, :], P), ALU.mult))
                ch.link(g.tensor_tensor(conv_t, u[:, :, 1:P + 1], last(taps[:, 1, :], P), ALU.mult))
                ch.link(g.tensor_tensor(conv_y, conv_y, conv_t, ALU.add))
                ch.link(g.tensor_tensor(conv_t, u[:, :, 2:P + 2], last(taps[:, 2, :], P), ALU.mult))
                ch.link(g.tensor_copy(u[:, :, 0:TAPS - 1], u[:, :, P:P + TAPS - 1]))
                g.tensor_tensor(conv_y, conv_y, conv_t, ALU.add).then_inc(y_ready, 1)
                wait(q_normed, i * HEADS + HEADS)
                if not first:
                    wait(qk_turned, i)
                rotate(q_raw[:, :, NOPE:], HEADS, i, q_rot, rope_t).then_inc(q_rot_ready, 1)

            tiles(pool, body)

            wait(tables_ready, 1)
            wait(zero_out, 16 * 4)
            pool.sem_inc(rows_free, 1)

            def gather(col):
                g.tensor_copy(pick_a, row_a[:, bass.ds(col, 1)]).then_inc(pick_ready, 1)
                g.tensor_copy(pick_b[0:SLOTS_B, :], row_b[0:SLOTS_B, bass.ds(col, 1)]).then_inc(pick_ready, 1)
                wait(pick_ready, col * 2)
                g.indirect_dma_start(xg_a, None, hf_dram, bass.IndirectOffsetOnAxis(
                    ap=pick_a, axis=0)).then_inc(gathered, 16)
                g.indirect_dma_start(xg_b[0:SLOTS_B, :], None, hf_dram, bass.IndirectOffsetOnAxis(
                    ap=pick_b[0:SLOTS_B, :], axis=0)).then_inc(gathered, 16)

            def scatter(col):
                wait(rows_ready, col * 4 + 4)
                g.tensor_copy(put_a, row_a[:, bass.ds(col, 1)]).then_inc(put_ready, 1)
                g.tensor_copy(put_b[0:SLOTS_B, :], row_b[0:SLOTS_B, bass.ds(col, 1)]).then_inc(put_ready, 1)
                wait(put_ready, col * 2 + 2)
                g.indirect_dma_start(acc_dram, bass.IndirectOffsetOnAxis(ap=put_a, axis=0),
                                     rows_a, None, compute_op=ALU.add).then_inc(scattered, 16)
                g.indirect_dma_start(acc_dram, bass.IndirectOffsetOnAxis(ap=put_b[0:SLOTS_B, :], axis=0),
                                     rows_b[0:SLOTS_B, :], None, compute_op=ALU.add).then_inc(scattered, 16)
                wait(scattered, col * 32 + 32)
                pool.sem_inc(rows_free, 1)

            n_tiles = pool.value_load(n_i[0:1, 0:1], min_val=1, max_val=MAX_TILES)
            wait(h_out, 16 * NT)
            wait(hf_out, 16 * NT)
            wait(idx_ready, 4)
            gather(1)
            g.memset(outT, 0.0).then_inc(zero_ready, 1)
            with expert_tiles(pool, n_tiles + 1) as t:
                with pool.If(t < n_tiles):
                    wait(idx_ready, t * 4 + 8)
                    wait(x_turned, t * 3 + 3)
                    wait(gathered, t * 32 + 32)
                    gather(t + 2)
                    scatter(t)
                with pool.Else():
                    with pool.If(t < n_tiles + 1):
                        scatter(t)

        @block.scalar
        def _(act):
            A = nc.scalar.activation
            act.wait_ge(consts_in, 16)
            eps = K["eps"]
            ms_x, std_x, rstd_x = stat[:, 0:1], stat[:, 1:2], stat[:, 2:3]
            c_ms, c_sd = stat[:, 3:5], stat[:, 5:7]
            kp_ss = stat[:, 9:10]
            hs, hsd = stat[:, 10:18], stat[:, 18:26]

            def norm_x(j, first):
                act.wait_ge(x_in, j * 16 + 16)
                if not first:
                    act.wait_ge(hn_turned, j)
                A(hn, xt, ACT.Square, scale=1.0 / D ** 0.5, accum_out=ms_x).then_inc(x_sq, 1)
                act.wait_ge(x_sq, j + 1)
                A(std_x, ms_x, ACT.Sqrt, bias=eps).then_inc(x_std, 1)
                act.wait_ge(x_rstd, j + 1)
                A(hn, xt, ACT.Copy, scale=rstd_x).then_inc(hn_ready, 1)

            def q_turned(j):
                act.wait_ge(qk_turned, j + 1)
                A(qT_n[:, :, bass.ds(j * P, P)], bank[0].rearrange("p (h n) -> p h n", h=HEADS),
                  ACT.Copy).then_inc(qT_ready, 1)
                A(qT_r[:, :, bass.ds(j * P, P)], bank[7][:, 0:2 * P].rearrange("p (h n) -> p h n", h=2),
                  ACT.Copy).then_inc(qT_ready, 1)
                A(kT_r[:, :, bass.ds(j * P, P)], bank[7][:, 2 * P:].rearrange("p (h n) -> p h n", h=2),
                  ACT.Copy).then_inc(qT_ready, 1)

            def body(i, first, last_tile):
                if not last_tile:
                    norm_x(i + 1, False)
                act.wait_ge(low_done, i + 1)
                if not first:
                    act.wait_ge(c_turned, i)
                    act.wait_ge(k_rot_ready, i)
                A(cn[:, 0:QL], bank[5][:, 0:QL], ACT.Square, scale=1.0 / QL ** 0.5,
                  accum_out=c_ms[:, 0:1]).then_inc(c_sq, 1)
                A(cn[:, QL:QL + KVL], bank[6][:, 0:KVL], ACT.Square, scale=1.0 / KVL ** 0.5,
                  accum_out=c_ms[:, 1:2]).then_inc(c_sq, 1)
                if not first:
                    act.wait_ge(kp_ready, i)
                A(cn[:, QL + KVL:LOW], bank[6][:, KVL:KVL + ROPE], ACT.Square,
                  accum_out=kp_ss).then_inc(c_sq, 1)
                act.wait_ge(c_sq, i * 3 + 3)
                A(c_sd, c_ms, ACT.Sqrt, bias=eps).then_inc(c_std, 1)
                if not first:
                    q_turned(i - 1)
                act.wait_ge(q_proj, i + 1)
                if not first:
                    act.wait_ge(q_rot_ready, i)
                for h in range(HEADS):
                    A(q_raw[:, h, :], bank[5 + h // 2][:, (h % 2) * QKH:(h % 2) * QKH + QKH], ACT.Square,
                      accum_out=hs[:, h:h + 1]).then_inc(head_sq, 1)
                act.wait_ge(kv_proj, i + 1)
                kv = [bank[7], bank[3]]
                for h in range(HEADS):
                    A(k_nope[:, h, :], kv[h // 2][:, (h % 2) * 256:(h % 2) * 256 + NOPE], ACT.Square,
                      accum_out=hs[:, HEADS + h:HEADS + h + 1]).then_inc(head_sq, 1)
                if first:
                    act.wait_ge(zero_out, 16 * 4)
                for c in range(2):
                    src = kv[c].rearrange("p (h s n) -> p h s n", h=2, s=2)[:, :, 1, :]
                    dst = v_sb[:, bass.ds(i, 1), c * 256:(c + 1) * 256].rearrange("p a (h n) -> p (a h) n", h=2)
                    A(dst, src, ACT.Copy).then_inc(v_ready, 1)
                act.wait_ge(head_sum, i + 1)
                A(hsd, hs, ACT.Sqrt, scale=1.0 / QKH, bias=eps).then_inc(head_std, 1)

            norm_x(0, True)
            tiles(act, body)
            q_turned(NT - 1)

            mx, sm = attn_stat[:, 0:32], attn_stat[:, 32:64]
            ms_h, sd_h = attn_stat[:, 96:104], attn_stat[:, 104:112]
            nm, = (attn_stat[:, 120:128],)
            n_evac = [0, 0]
            for kind, n in steps:
                if kind == "S":
                    i = n // HEADS
                    L = (i + 1) * P
                    act.wait_ge(s_max, n + 1)
                    if n >= 2:
                        act.wait_ge(turn_a, use_a[("TP", n - 2)])
                        if ("TP", n - 2) in use_b:
                            act.wait_ge(turn_b, use_b[("TP", n - 2)])
                    sc = psum[:, (n % 2) * 1024:(n % 2) * 1024 + L]
                    A(prob[n % 2][:, 0:L], sc, ACT.Exp, scale=SCALE, bias=mx[:, n:n + 1],
                      accum_out=sm[:, n:n + 1]).then_inc(exp_done, 1)
                if kind == "TP":
                    i = n // HEADS
                    act.wait_ge(turn_a, use_a[(kind, n)])
                    if n >= 2:
                        act.wait_ge(pv_done, n - 1)
                    m = min(i + 1, 4)
                    A(probT[n % 2][:, 0:m, :], bank[4][:, 0:m * P].rearrange("p (k n) -> p k n", k=m),
                      ACT.Copy).then_inc(turn_a_read, 1)
                if kind == "OT":
                    act.wait_ge(turn_a, use_a[(kind, n)])
                    if n:
                        act.wait_ge(wo_done, 2 * n)
                    A(attnT, bank[4].rearrange("p (k n) -> p k n", k=HEADS), ACT.Copy).then_inc(turn_a_read, 1)
                if kind == "HT":
                    act.wait_ge(turn_a, use_a[(kind, n)])
                    if n:
                        act.wait_ge(rt_done, n)
                    A(hfT[:, 0:4, :], bank[4].rearrange("p (k n) -> p k n", k=4), ACT.Copy).then_inc(turn_a_read, 1)
                if kind == "WO" and n % 2:
                    i = n // 2
                    act.wait_ge(h_ready, n + 1)
                    if i:
                        act.wait_ge(turn_a, use_a[("HT", i - 1)])
                        act.wait_ge(turn_b, use_b[("HT", i - 1)])
                        act.wait_ge(hf_out, 16 * i)
                    A(hf, h_sb[i % 2], ACT.Square, scale=1.0 / D ** 0.5, accum_out=ms_h[:, i:i + 1]).then_inc(h_sq, 1)
                    act.wait_ge(h_sq, i + 1)
                    A(sd_h[:, i:i + 1], ms_h[:, i:i + 1], ACT.Sqrt, bias=eps).then_inc(h_std, 1)
                if kind == "RT":
                    act.wait_ge(top_ready, n + 1)
                    A(em, lg, ACT.Exp, bias=nm[:, n:n + 1]).then_inc(e_ready, 1)

            act.wait_ge(tables_ready, 1)
            act.wait_ge(zero_ready, 3)
            act.sem_inc(outT_ready, 8)
            n_tiles = act.value_load(n_i[0:1, 0:1], min_val=1, max_val=MAX_TILES)

            def sigmoid(t, c):
                act.wait_ge(gu_read, t * 16 + 2 * c + 5)
                A(sg[:, c % 2, :], g_c[:, c % 2, :], ACT.Sigmoid, scale=ALPHA).then_inc(sig_ready, 1)

            def flush_rows(col, part_b):
                pn, rows, gates = (SLOTS_B, rows_b, gate_b) if part_b else (P, rows_a, gate_a)
                act.wait_ge(rows_turned, col * 2 + (2 if part_b else 1))
                if not part_b:
                    act.wait_ge(rows_free, col + 1)
                for hlf in range(2):
                    A(rows[0:pn, hlf * 512:(hlf + 1) * 512], bank[5 + hlf][0:pn, :], ACT.Copy,
                      scale=gates[0:pn, bass.ds(col, 1)]).then_inc(rows_ready, 1)

            with expert_tiles(act, n_tiles + 1) as t:
                with act.If(t < n_tiles):
                    e = act.value_load(te_i[0:1, bass.ds(t, 1)], min_val=0, max_val=E - 1)
                    for c in range(NC):
                        sigmoid(t, c)
                        if c == 1:
                            flush_rows(t, False)
                        if c == 2:
                            flush_rows(t, True)
                    act.wait_ge(down_done, t * 4 + 4)
                    act.wait_ge(rows_turned, t * 2 + 2)
                    for d in range(KD):
                        A(outT[:, d, :], bank[2 + d // 3][:, (d % 3) * SLOTS:(d % 3 + 1) * SLOTS], ACT.Identity,
                          bias=bdT[:, d, bass.ds(e, 1)]).then_inc(outT_ready, 1)
                with act.Else():
                    with act.If(t < n_tiles + 1):
                        flush_rows(t, False)
                        flush_rows(t, True)

        @block.tensor
        def _(pe):
            mm, tr = nc.tensor.matmul, nc.tensor.transpose
            pe.wait_ge(consts_in, 16)

            def turn_hn(j):
                pe.wait_ge(hn_ready, j + 1)
                for k in range(KD):
                    ins = tr(bank[k // 4][:, (k % 4) * P:(k % 4 + 1) * P], hn[:, k * P:(k + 1) * P], ident)
                ins.then_inc(hn_turned, 1)

            def turn_qk(j):
                pe.wait_ge(q_rot_ready, j + 1)
                pe.wait_ge(k_rot_ready, j + 1)
                pe.wait_ge(v_ready, j * 2 + 2)
                for h in range(HEADS):
                    tr(bank[0][:, h * P:(h + 1) * P], q_raw[:, h, 0:NOPE], ident)
                for h in range(HEADS):
                    tr(bank[1][:, h * P:(h + 1) * P], k_nope[:, h, :], ident)
                for c in range(2):
                    tr(bank[7][:, c * P:(c + 1) * P], q_rot[:, c * P:(c + 1) * P], ident)
                for c in range(2):
                    ins = tr(bank[7][:, (2 + c) * P:(3 + c) * P], k_rot[:, c * P:(c + 1) * P], ident)
                ins.then_inc(qk_turned, 1)

            def channels(bk, col):
                for f in range(NF):
                    for k in range(KD):
                        ins = mm(bk[:, f * P:(f + 1) * P], w_in[:, k, col + f * P:col + (f + 1) * P], hnT[:, k, :],
                                 start=(k == 0), stop=(k == KD - 1))
                return ins

            def body(i, first, last_tile):
                pe.wait_ge(hnT_ready, i * 2 + 2)
                if first:
                    pe.wait_ge(w_low_in, 16)
                else:
                    pe.wait_ge(u_ready, i)
                    channels(bank[2], CONV)
                    pe.wait_ge(q_normed, i * HEADS)
                for k in range(KD):
                    mm(bank[5][:, 0:QL], hnT[:, k, :], w_in[:, k, 3 * CONV:3 * CONV + QL],
                       start=(k == 0), stop=(k == KD - 1))
                for k in range(KD):
                    ins = mm(bank[6][:, 0:KVL + ROPE], hnT[:, k, :], w_in[:, k, 3 * CONV + QL:],
                             start=(k == 0), stop=(k == KD - 1))
                ins.then_inc(low_done, 1)
                if first:
                    pe.wait_ge(w_cx_in, 16)
                    channels(bank[2], CONV)
                else:
                    turn_qk(i - 1)
                    pe.wait_ge(k_normed, i * HEADS)
                channels(bank[3], 2 * CONV).then_inc(cx_done, 1)
                pe.wait_ge(c_ready, i * 3 + 3)
                if not first:
                    pe.wait_ge(qT_ready, i * 3)
                    pe.wait_ge(kT_ready, i)
                for c in range(NCQ):
                    tr(bank[0][:, c * P:(c + 1) * P], cn[:, c * P:(c + 1) * P], ident)
                for c in range(NCKV):
                    ins = tr(bank[1][:, c * P:(c + 1) * P], cn[:, QL + c * P:QL + (c + 1) * P], ident)
                ins.then_inc(c_turned, 1)
                if first:
                    pe.wait_ge(w_b_in, 16)
                else:
                    pe.wait_ge(conv_done, i)
                channels(bank[4], 0).then_inc(b_done, 1)
                pe.wait_ge(cT_ready, i * 2 + 2)
                if not last_tile:
                    turn_hn(i + 1)
                if first:
                    pe.wait_ge(w_uq_in, 16)
                    pe.wait_ge(w_ukv_in, 16)
                for c in range(2):
                    for k in range(NCQ):
                        ins = mm(bank[5 + c][:, 0:2 * QKH], cT[:, k, :], w_uq[:, k, c * 2 * QKH:(c + 1) * 2 * QKH],
                                 start=(k == 0), stop=(k == NCQ - 1))
                ins.then_inc(q_proj, 1)
                pe.wait_ge(u_ready, i + 1)
                for c, bk in enumerate((bank[7], bank[3])):
                    for k in range(NCKV):
                        ins = mm(bk, cT[:, NCQ + k, :], w_ukv[:, k, c * 512:(c + 1) * 512],
                                 start=(k == 0), stop=(k == NCKV - 1))
                ins.then_inc(kv_proj, 1)

            turn_hn(0)
            tiles(pe, body)
            turn_qk(NT - 1)

            pe.wait_ge(bias_in, 16 * 3)
            pe.wait_ge(qT_ready, 3 * NT)
            pe.wait_ge(kT_ready, NT)
            for c in range(2 * NC):
                tr(bank[7][:, c * E:(c + 1) * E], bias_rows[0:E, c * P:(c + 1) * P], ident[0:E, 0:E])
            for c in range(KD):
                ins = tr(bank[6][:, c * E:(c + 1) * E], bias_rows[0:E, 2 * FF + c * P:2 * FF + (c + 1) * P],
                         ident[0:E, 0:E])
            ins.then_inc(bias_turned, 1)
            pe.wait_ge(bias_ready, 2)
            pe.wait_ge(conv_done, NT)
            for kind, n in steps:
                if kind == "S":
                    i, h = n // HEADS, n % HEADS
                    if n >= 2:
                        pe.wait_ge(exp_done, n - 1)
                    r0 = (h % 2) * ROPE
                    for c in range(0, (i + 1) * P, 512):
                        w = min(512, (i + 1) * P - c)
                        dst = bank[(n % 2) * 2 + c // 512][:, 0:w]
                        mm(dst, qT_n[:, h, i * P:(i + 1) * P], kT_n[:, h, c:c + w], start=True, stop=False)
                        ins = mm(dst, qT_r[r0:r0 + ROPE, h // 2, i * P:(i + 1) * P],
                                 kT_r[r0:r0 + ROPE, h // 2, c:c + w], start=False, stop=True)
                    ins.then_inc(s_done, 1)
                if kind in ("TP", "OT", "HT"):
                    ua = use_a[(kind, n)]
                    if ua > 1:
                        pe.wait_ge(turn_a_read, ua - 1)
                    if kind == "TP":
                        pe.wait_ge(exp_done, n + 1)
                        src = [prob[n % 2][:, k * P:(k + 1) * P] for k in range(n // HEADS + 1)]
                    if kind == "OT":
                        pe.wait_ge(o_ready, HEADS * (n + 1))
                        src = [o_sb[:, k * P:(k + 1) * P] for k in range(HEADS)]
                    if kind == "HT":
                        pe.wait_ge(hf_ready, n + 1)
                        src = [hf[:, k * P:(k + 1) * P] for k in range(KD)]
                    for k, s in enumerate(src[0:4]):
                        ins = tr(bank[4][:, k * P:(k + 1) * P], s, ident)
                    ins.then_inc(turn_a, 1)
                    if len(src) > 4:
                        ub = use_b[(kind, n)]
                        if ub > 1:
                            pe.wait_ge(turn_b_read, ub - 1)
                        for k, s in enumerate(src[4:]):
                            ins = tr(bank[5][:, k * P:(k + 1) * P], s, ident)
                        ins.then_inc(turn_b, 1)
                if kind == "PV":
                    i, h = n // HEADS, n % HEADS
                    pe.wait_ge(turn_a_read, use_a[("TP", n)])
                    if n:
                        pe.wait_ge(o_ready, n)
                    for k in range(i + 1):
                        if k == 4:
                            pe.wait_ge(turn_b_read, use_b[("TP", n)])
                        ins = mm(bank[6][:, h * VH:(h + 1) * VH], probT[n % 2][:, k, :],
                                 v_sb[:, k, h * VH:(h + 1) * VH], start=(k == 0), stop=(k == i))
                    ins.then_inc(pv_done, 1)
                if kind == "WO":
                    i, c = n // 2, n % 2
                    if n == 0:
                        pe.wait_ge(w_o_in, 16)
                    if c == 0:
                        pe.wait_ge(turn_a_read, use_a[("OT", i)])
                        if i:
                            pe.wait_ge(lg_read, i)
                    if n:
                        pe.wait_ge(h_ready, n)
                    for k in range(2 * NF):
                        lhs = convT[:, k, i * P:(i + 1) * P] if k < NF else attnT[:, k - NF, :]
                        ins = mm(bank[7], lhs, w_o[:, k, c * 512:(c + 1) * 512], start=(k == 0), stop=(k == 2 * NF - 1))
                    ins.then_inc(wo_done, 1)
                if kind == "RT":
                    pe.wait_ge(turn_a_read, use_a[("HT", n)])
                    pe.wait_ge(turn_b_read, use_b[("HT", n)])
                    pe.wait_ge(w_r_in, 16)
                    pe.wait_ge(h_ready, RT_H[n])
                    if n:
                        pe.wait_ge(lg_read, n)
                    for k in range(KD):
                        mm(bank[7][:, 0:E], hfT[:, k, :], w_r[:, k, :], start=(k == 0), stop=False)
                    mm(bank[7][:, 0:E], ones[0:1, :], br_row[0:1, :], start=False, stop=True).then_inc(rt_done, 1)

            pe.wait_ge(gate_ready, NT)
            masks = mask.rearrange("p t e -> p (t e)")
            mm(bank[0][:, 0:NT * E], K["before"], masks, start=True, stop=True)
            mm(bank[1][:, 0:NT * E], ones, masks, start=True, stop=True).then_inc(rank_mm, 1)

            pe.wait_ge(tab_ready, 1)
            mm(bank[2][:, 0:P], spread, ident, start=True, stop=True)
            mm(bank[2][0:1, 128:128 + P], tab[:, 0:1], ident, start=True, stop=True)
            mm(bank[2][0:1, 256:256 + P], tab[:, 2:3], ident, start=True, stop=True).then_inc(tab_turned, 1)

            def index(t):
                pe.wait_ge(sel_ready, t + 1)
                e = pe.value_load(te_i[0:1, bass.ds(t, 1)], min_val=0, max_val=E - 1)
                for c0, cn_, dst in ((0, P, bank[7][:, 496:496 + ROUTE]),
                                     (P, SLOTS_B, bank[7][0:SLOTS_B, 504:504 + ROUTE])):
                    for k in range(NT):
                        rhs = route[:, k, bass.ds(e, 1), :].rearrange("p a c -> p (a c)")
                        ins = mm(dst, sel[:, k, c0:c0 + cn_], rhs, start=(k == 0), stop=(k == NT - 1))
                ins.then_inc(idx_done, 1)

            def turn_x(t):
                pe.wait_ge(gathered, t * 32 + 32)
                for k in range(KD):
                    bk, col = bank[5 + k // 3], (k % 3) * SLOTS
                    tr(bk[:, col:col + P], xg_a[:, k * P:(k + 1) * P], ident)
                    ins = tr(bk[:, col + P:col + SLOTS], xg_b[0:SLOTS_B, k * P:(k + 1) * P],
                             ident[0:SLOTS_B, 0:SLOTS_B])
                    if k % 3 == 2 or k == KD - 1:
                        ins.then_inc(x_turned, 1)

            def turn_rows(col, part_b):
                c0, pn = (P, SLOTS_B) if part_b else (0, P)
                if part_b:
                    pe.wait_ge(rows_ready, col * 4 + 2)
                else:
                    pe.wait_ge(outT_ready, col * 8 + 8)
                for d in range(KD):
                    ins = tr(bank[5 + d // 4][0:pn, (d % 4) * P:(d % 4 + 1) * P], outT[:, d, c0:c0 + pn], ident)
                ins.then_inc(rows_turned, 1)

            def gate_up(t, c, width):
                q, cc = c // 2, (c % 2) * P
                bk = bank[c % 2]
                pe.wait_ge(gu_read, t * 16 + 2 * c + 2)
                if c % 2 == 0:
                    pe.wait_ge(w_exp_in[2 * q], t * 16 + 16)
                for k in range(KD):
                    mm(bk[:, 0:width], w_gu[2 * q][:, k, cc:cc + P], xT[:, k, 0:width], start=(k == 0), stop=(k == KD - 1))
                if c % 2 == 0:
                    pe.wait_ge(w_exp_in[2 * q + 1], t * 16 + 16)
                for k in range(KD):
                    ins = mm(bk[:, SLOTS:SLOTS + width], w_gu[2 * q + 1][:, k, cc:cc + P], xT[:, k, 0:width],
                             start=(k == 0), stop=(k == KD - 1))
                ins.then_inc(gu_done, 1)

            def down(t, q, width):
                pe.wait_ge(w_exp_in[8 + q], t * 16 + 16)
                pe.wait_ge(act_ready, t * 8 + 2 * q + 2)
                if q == 0:
                    pe.wait_ge(outT_ready, t * 8 + 8)
                for kk in range(2):
                    for d in range(KD):
                        ins = mm(bank[2 + d // 3][:, (d % 3) * SLOTS:(d % 3) * SLOTS + width],
                                 w_dn[q][:, kk, d * P:(d + 1) * P], actT[:, 2 * q + kk, 0:width],
                                 start=(q == 0 and kk == 0 and d % 3 == 0), stop=(q == 3 and kk == 1),
                                 skip_group_check=True)
                ins.then_inc(down_done, 1)

            pe.wait_ge(route_ready, 1)
            n_tiles = pe.value_load(n_i[0:1, 0:1], min_val=1, max_val=MAX_TILES)
            index(0)
            turn_x(0)
            def expert_tile(t, width):
                pe.wait_ge(xT_ready, t * 3 + 3)
                gate_up(t, 0, width)
                gate_up(t, 1, width)
                turn_rows(t, False)
                index(t + 1)
                gate_up(t, 2, width)
                turn_rows(t, True)
                for c in range(3, NC):
                    gate_up(t, c, width)
                pe.wait_ge(rows_ready, t * 4 + 4)
                pe.wait_ge(idx_ready, t * 4 + 8)
                turn_x(t + 1)
                for q in range(4):
                    down(t, q, width)

            with expert_tiles(pe, n_tiles + 1) as t:
                tokens = pe.value_load(held_i[0:1, bass.ds(t, 1)])

                def narrowest(widths):
                    if len(widths) > 1:
                        half = len(widths) // 2
                        with pe.If(tokens < widths[half - 1] + 1):
                            narrowest(widths[:half])
                        with pe.Else():
                            narrowest(widths[half:])
                    elif widths[0]:
                        expert_tile(t, widths[0])
                    else:
                        with pe.If(t < n_tiles + 1):
                            pe.wait_ge(xT_ready, t * 3 + 3)
                            turn_rows(t, False)
                            turn_rows(t, True)

                narrowest([0] + WIDTHS)

        @block.vector
        def _(dve):
            V = nc.vector
            ch = Chain(dve, dve_chain)
            dve.wait_ge(consts_in, 16)
            dve.wait_ge(g_mix_in, 16)
            ms_x, std_x, rstd_x = stat[:, 0:1], stat[:, 1:2], stat[:, 2:3]
            c_sd, c_rs, kp_ss = stat[:, 5:7], stat[:, 7:9], stat[:, 9:10]
            hs, hsd, hrs = stat[:, 10:18], stat[:, 18:26], stat[:, 26:34]

            def rstd(j):
                dve.wait_ge(x_std, j + 1)
                V.reciprocal(rstd_x, std_x).then_inc(x_rstd, 1)

            def hnT_out(j, first):
                dve.wait_ge(hn_turned, j + 1)
                if not first:
                    dve.wait_ge(b_done, j)
                for c in range(2):
                    V.tensor_tensor(hnT[:, 4 * c:4 * c + 4, :], bank[c].rearrange("p (k n) -> p k n", k=4),
                                    last(g_mix[:, 4 * c:4 * c + 4], P), ALU.mult).then_inc(hnT_ready, 1)

            def kT_out(j):
                dve.wait_ge(qk_turned, j + 1)
                V.tensor_copy(kT_n[:, :, bass.ds(j * P, P)],
                              bank[1].rearrange("p (h n) -> p h n", h=HEADS)).then_inc(kT_ready, 1)

            def body(i, first, last_tile):
                if not last_tile:
                    rstd(i + 1)
                if first:
                    dve.wait_ge(small_in, 16 * 7)
                dve.wait_ge(c_std, i + 1)
                V.reciprocal(c_rs, c_sd).then_inc(c_rstd, 1)
                dve.wait_ge(c_rstd, i + 1)
                V.tensor_scalar(cn[:, 0:QL], bank[5][:, 0:QL], c_rs[:, 0:1], None, ALU.mult).then_inc(c_ready, 1)
                V.tensor_scalar(cn[:, QL:QL + KVL], bank[6][:, 0:KVL], c_rs[:, 1:2], None, ALU.mult).then_inc(c_ready, 1)
                V.tensor_tensor(cn[:, QL + KVL:], bank[6][:, KVL:KVL + ROPE], gk_row[:, NOPE:], ALU.mult).then_inc(c_ready, 1)
                if not first:
                    kT_out(i - 1)
                dve.wait_ge(cx_done, i + 1)
                if not first:
                    dve.wait_ge(y_ready, i)
                ch.at(i)
                ch.link(V.tensor_copy(c_gate, bank[2].rearrange("p (f n) -> p f n", f=NF)))
                V.tensor_tensor(u[:, :, TAPS - 1:], c_gate, bank[3].rearrange("p (f n) -> p f n", f=NF),
                                ALU.mult).then_inc(u_ready, 1)
                dve.wait_ge(c_turned, i + 1)
                if not first:
                    dve.wait_ge(kv_proj, i)
                V.tensor_tensor(cT[:, 0:NCQ, :], bank[0][:, 0:QL].rearrange("p (k n) -> p k n", k=NCQ),
                                last(g_q[:, 0:NCQ], P), ALU.mult).then_inc(cT_ready, 1)
                V.tensor_tensor(cT[:, NCQ:, :], bank[1][:, 0:KVL].rearrange("p (k n) -> p k n", k=NCKV),
                                last(g_q[:, NCQ:], P), ALU.mult).then_inc(cT_ready, 1)
                dve.wait_ge(b_done, i + 1)
                dve.wait_ge(y_ready, i + 1)
                V.tensor_tensor(convT[:, :, bass.ds(i * P, P)], bank[4].rearrange("p (f n) -> p f n", f=NF),
                                conv_y, ALU.mult).then_inc(conv_done, 1)
                if not last_tile:
                    hnT_out(i + 1, False)
                dve.wait_ge(head_sq, i * 8 + 8)
                V.tensor_scalar(hs[:, HEADS:], hs[:, HEADS:], kp_ss, None, ALU.add).then_inc(head_sum, 1)
                dve.wait_ge(head_std, i + 1)
                V.reciprocal(hrs, hsd).then_inc(head_rstd, 1)
                dve.wait_ge(head_rstd, i + 1)
                for h in range(HEADS):
                    V.scalar_tensor_tensor(q_raw[:, h, :], bank[5 + h // 2][:, (h % 2) * QKH:(h % 2) * QKH + QKH],
                                           hrs[:, h:h + 1], gq_row[:], ALU.mult, ALU.mult).then_inc(q_normed, 1)
                kv = [bank[7], bank[3]]
                dve.wait_ge(v_ready, i * 2 + 2)
                for h in range(HEADS):
                    V.scalar_tensor_tensor(k_nope[:, h, :], kv[h // 2][:, (h % 2) * 256:(h % 2) * 256 + NOPE],
                                           hrs[:, HEADS + h:HEADS + h + 1], gk_row[:, 0:NOPE],
                                           ALU.mult, ALU.mult).then_inc(k_normed, 1)
                dve.wait_ge(kp_ready, i + 1)
                V.tensor_tensor(k_rot.rearrange("p (h n) -> p h n", h=HEADS), mid(kp_rot, HEADS),
                                last(hrs[:, HEADS:], ROPE), ALU.mult).then_inc(k_rot_ready, 1)

            rstd(0)
            hnT_out(0, True)
            tiles(dve, body)
            kT_out(NT - 1)

            ch.at(NT)
            mx, sm, rs = attn_stat[:, 0:32], attn_stat[:, 32:64], attn_stat[:, 64:96]
            sd_h, rs_h = attn_stat[:, 104:112], attn_stat[:, 112:120]
            nm = attn_stat[:, 120:128]
            dve.wait_ge(bias_turned, 1)
            V.tensor_copy(bguT, bank[7].rearrange("p (c e) -> p c e", e=E)).then_inc(bias_ready, 1)
            V.tensor_copy(bdT, bank[6][:, 0:KD * E].rearrange("p (c e) -> p c e", e=E)).then_inc(bias_ready, 1)
            for kind, n in steps:
                if kind == "S":
                    i = n // HEADS
                    L = (i + 1) * P
                    sc = psum[:, (n % 2) * 1024:(n % 2) * 1024 + L]
                    dve.wait_ge(s_done, n + 1)
                    ch.link(V.memset(sc[0:CHUNK, L - CHUNK:L], NEG))
                    ch.link(V.reduce_max(mx[:, n:n + 1], sc, AX_X))
                    V.tensor_scalar(mx[:, n:n + 1], mx[:, n:n + 1], -SCALE, None, ALU.mult).then_inc(s_max, 1)
                if (kind, n) in use_b:
                    dve.wait_ge(turn_b, use_b[(kind, n)])
                    src = bank[5]
                    if kind == "TP":
                        m = n // HEADS + 1 - 4
                        if n >= 2:
                            dve.wait_ge(pv_done, n - 1)
                        V.tensor_copy(probT[n % 2][:, 4:4 + m, :],
                                      src[:, 0:m * P].rearrange("p (k n) -> p k n", k=m)).then_inc(turn_b_read, 1)
                    else:
                        if n:
                            dve.wait_ge(rt_done, n)
                        V.tensor_copy(hfT[:, 4:8, :], src.rearrange("p (k n) -> p k n", k=4)).then_inc(turn_b_read, 1)
                if kind == "PV":
                    i, h = n // HEADS, n % HEADS
                    dve.wait_ge(pv_done, n + 1)
                    ch.link(V.reciprocal(rs[:, n:n + 1], sm[:, n:n + 1]))
                    if h == 0 and i:
                        dve.wait_ge(turn_a, use_a[("OT", i - 1)])
                    V.tensor_scalar(o_sb[:, h * VH:(h + 1) * VH], bank[6][:, h * VH:(h + 1) * VH],
                                    rs[:, n:n + 1], None, ALU.mult).then_inc(o_ready, 1)
                if kind == "WO":
                    i, c = n // 2, n % 2
                    dve.wait_ge(wo_done, n + 1)
                    dve.wait_ge(hx_in[i % 2], 16 * (i // 2 + 1))
                    V.tensor_tensor(h_sb[i % 2][:, c * 512:(c + 1) * 512], h_sb[i % 2][:, c * 512:(c + 1) * 512],
                                    bank[7], ALU.add).then_inc(h_ready, 1)
                    if c:
                        if i == 0:
                            dve.wait_ge(row_in, 16)
                        dve.wait_ge(h_std, i + 1)
                        ch.link(V.reciprocal(rs_h[:, i:i + 1], sd_h[:, i:i + 1]))
                        V.scalar_tensor_tensor(hf, h_sb[i % 2], rs_h[:, i:i + 1], gf_row,
                                               ALU.mult, ALU.mult).then_inc(hf_ready, 1)
                if kind == "RT":
                    dve.wait_ge(rt_done, n + 1)
                    V.tensor_copy(lg, bank[7][:, 0:E]).then_inc(lg_read, 1)
                    dve.wait_ge(lg_read, n + 1)
                    ch.link(V.max(top8, lg))
                    V.tensor_scalar(nm[:, n:n + 1], top8[:, 0:1], -1.0, None, ALU.mult).then_inc(top_ready, 1)
                    ch.link(V.max_index(idx8, top8, lg))
                    ch.link(V.tensor_copy(idxf, idx8))
                    ch.link(V.tensor_scalar(mask[:, n, :], K["expert"], idxf[:, 0:1], None, ALU.is_equal))
                    for k in range(1, TOPK):
                        ch.link(V.scalar_tensor_tensor(mask[:, n, :], K["expert"], idxf[:, k:k + 1], mask[:, n, :],
                                                       ALU.is_equal, ALU.add))
                    dve.wait_ge(e_ready, n + 1)
                    ch.link(V.tensor_tensor(em, em, mask[:, n, :], ALU.mult))
                    ch.link(V.reduce_sum(gsum[:, 0:1], em, AX_X))
                    ch.link(V.reciprocal(gsum[:, 1:2], gsum[:, 0:1]))
                    V.tensor_scalar(gate[:, n, :], em, gsum[:, 1:2], None, ALU.mult).then_inc(gate_ready, 1)

            dve.wait_ge(rank_mm, 1)
            dve.wait_ge(gate_ready, NT)
            dve.wait_ge(hf_out, 16 * NT)
            dve.wait_ge(h_out, 16 * NT)
            ch.link(V.memset(off[:, 0, :], 0.0))
            for t in range(NT):
                ch.link(V.tensor_tensor(off[:, t + 1, :], off[:, t, :], bank[1][:, t * E:(t + 1) * E], ALU.add))
            ch.link(V.tensor_tensor(rank, off[:, 0:NT, :], bank[0][:, 0:NT * E].rearrange("p (t e) -> p t e", t=NT), ALU.add))
            ch.link(V.scalar_tensor_tensor(rank, rank, 1.0, mask, ALU.add, ALU.mult))
            ch.link(V.tensor_scalar(rank, rank, -1.0, None, ALU.add))
            count = off[:, NT, :]
            ch.link(V.tensor_scalar(used, count, 0.0, None, ALU.is_gt))
            for j in range(1, LEVELS):
                ch.link(V.scalar_tensor_tensor(used, count, float(j * SLOTS), used, ALU.is_gt, ALU.add))
            ch.link(V.tensor_copy(cum[:, 0, :], used))
            src, s = 0, 1
            while s < E:
                V.tensor_copy(cum[:, 1 - src, 0:s], cum[:, src, 0:s])
                ch.link(V.tensor_tensor(cum[:, 1 - src, s:], cum[:, src, s:], cum[:, src, 0:E - s], ALU.add))
                src, s = 1 - src, 2 * s
            total = cum[:, src, :]
            tile_no = K["tokp"]
            ch.link(V.tensor_tensor(first_t, total, used, ALU.subtract))
            V.tensor_scalar(past_e, total, tile_no, None, ALU.is_le)
            ch.link(V.tensor_scalar(at_e, first_t, tile_no, None, ALU.is_le))
            V.tensor_reduce(tab[:, 0:1], past_e, AX_X, ALU.add)
            V.tensor_tensor(prod[:, 0, :], past_e, used, ALU.mult)
            ch.link(V.tensor_tensor(at_e, at_e, past_e, ALU.subtract))
            V.tensor_reduce(tab[:, 1:2], prod[:, 0, :], AX_X, ALU.add)
            ch.link(V.tensor_tensor(prod[:, 1, :], at_e, count, ALU.mult))
            ch.link(V.tensor_reduce(tab[:, 2:3], prod[:, 1, :], AX_X, ALU.add))
            V.tensor_scalar(tab[:, 0:1], tab[:, 0:1], float(E - 1), None, ALU.min)
            ch.link(V.tensor_scalar(tab[:, 1:2], tab[:, 1:2], tile_no, -float(SLOTS), ALU.subtract, ALU.mult))
            V.tensor_tensor(tab[:, 2:3], tab[:, 2:3], tab[:, 1:2], ALU.subtract)
            V.tensor_scalar(spread, ones, tab[:, 1:2], None, ALU.mult).then_inc(tab_ready, 1)
            dve.wait_ge(tab_turned, 1)
            V.tensor_copy(n_i, total[:, E - 1:E])
            V.tensor_copy(jt_f, bank[2][:, 0:TABLE])
            V.tensor_copy(held_i[0:1, :], bank[2][0:1, 256:256 + TABLE])
            ch.link(V.tensor_copy(te_i[0:1, :], bank[2][0:1, 128:128 + TABLE]))
            V.engine_nop().then_inc(tables_ready, 1)
            flat = "p t e -> p (t e)"
            V.tensor_copy(route[:, :, :, 0].rearrange(flat), K["tokp"].to_broadcast([P, NT * E]))
            V.tensor_copy(route[:, :, :, 1], last(K["tilebase"], E))
            V.memset(route[:, :, :, 2], 1.0)
            ch.link(V.tensor_copy(route[:, :, :, 3], gate))
            ch.link(V.tensor_tensor(res_t, gate, route[:, :, :, 3], ALU.subtract))
            ch.link(V.tensor_copy(route[:, :, :, 4], res_t))
            ch.link(V.tensor_tensor(res_t, res_t, route[:, :, :, 4], ALU.subtract))
            ch.link(V.tensor_copy(route[:, :, :, 5], res_t))
            V.tensor_copy(row_a[:, 0:1], K["pad"][:, 0:1])
            V.tensor_copy(row_b[:, 0:1], K["pad"][:, 1:2])
            V.memset(gate_a[:, 0:1], 0.0)
            V.memset(gate_b[:, 0:1], 0.0).then_inc(route_ready, 1)

            dve.wait_ge(tables_ready, 1)
            dve.wait_ge(route_ready, 1)
            n_tiles = dve.value_load(n_i[0:1, 0:1], min_val=1, max_val=MAX_TILES)
            D_LINKS = 1 + 2 * 2 + NC
            start = ch.base + ch.n
            dve.sem_inc(gu_read, 4)

            def select(t):
                e = dve.value_load(te_i[0:1, bass.ds(t, 1)], min_val=0, max_val=E - 1)
                r = rank[:, :, bass.ds(e, 1)].rearrange("p t a -> p (t a)")
                ch.link(V.tensor_scalar(rl, r, jt_f[:, bass.ds(t, 1)], None, ALU.subtract))
                V.tensor_tensor(sel, mid(K["slot"], NT), last(rl, SLOTS), ALU.is_equal).then_inc(sel_ready, 1)

            def index_out(t):
                dve.wait_ge(idx_done, t + 1)
                for pn, col, ix, rows, gates, c in ((P, 496, ix_a, row_a, gate_a, 0),
                                                    (SLOTS_B, 504, ix_b, row_b, gate_b, 1)):
                    ch.link(V.tensor_copy(ix[0:pn, 0:ROUTE], bank[7][0:pn, col:col + ROUTE]))
                    ch.link(V.tensor_scalar(ix[0:pn, ROUTE:ROUTE + 1], ix[0:pn, 2:3], K["npad"][0:pn, c:c + 1],
                                            K["pad"][0:pn, c:c + 1], ALU.mult, ALU.add))
                    V.tensor_scalar(rows[0:pn, bass.ds(t + 1, 1)], ix[0:pn, 0:1], ix[0:pn, 1:2],
                                    ix[0:pn, ROUTE:ROUTE + 1], ALU.add, ALU.add).then_inc(idx_ready, 1)
                    V.tensor_reduce(gates[0:pn, bass.ds(t + 1, 1)], ix[0:pn, 3:6], AX_X, ALU.add).then_inc(idx_ready, 1)

            def xT_out(t):
                for r in range(3):
                    m = 3 if r < 2 else KD - 6
                    dve.wait_ge(x_turned, t * 3 + r + 1)
                    V.tensor_copy(xT[:, 3 * r:3 * r + m, :],
                                  bank[5 + r][:, 0:m * SLOTS].rearrange("p (k n) -> p k n", k=m)).then_inc(xT_ready, 1)

            def clamp(t, e, c):
                bk, b = bank[c % 2], c % 2
                dve.wait_ge(gu_done, t * NC + c + 1)
                V.tensor_scalar(g_c[:, b, :], bk[:, 0:SLOTS], bguT[:, c, bass.ds(e, 1)], LIMIT,
                                ALU.add, ALU.min).then_inc(gu_read, 1)
                V.tensor_scalar(u_c[:, b, :], bk[:, SLOTS:2 * SLOTS], bguT[:, NC + c, bass.ds(e, 1)], -LIMIT,
                                ALU.add, ALU.max).then_inc(gu_read, 1)

            def product(t, c):
                b = c % 2
                dve.wait_ge(gu_read, t * 16 + 2 * c + 6)
                V.tensor_scalar(u2_t, u_c[:, b, :], LIMIT, 1.0, ALU.min, ALU.add)
                dve.wait_ge(sig_ready, t * NC + c + 1)
                ch.link(V.tensor_tensor(gs_t, g_c[:, b, :], sg[:, b, :], ALU.mult))
                ins = V.tensor_tensor(actT[:, c, :], u2_t, gs_t, ALU.mult)
                ins.then_inc(act_ready, 1)
                dve.wait_ge(act_ready, t * NC + c + 1)

            ch.at(start)
            select(0)
            index_out(0)
            xT_out(0)
            start = ch.base + ch.n
            with expert_tiles(dve, n_tiles) as t:
                with dve.If(t < n_tiles):
                    ch.at(t * D_LINKS + start)
                    e = dve.value_load(te_i[0:1, bass.ds(t, 1)], min_val=0, max_val=E - 1)
                    select(t + 1)
                    clamp(t, e, 0)
                    clamp(t, e, 1)
                    product(t, 0)
                    index_out(t + 1)
                    for c in range(2, NC):
                        clamp(t, e, c)
                        product(t, c - 1)
                    product(t, NC - 1)
                    xT_out(t + 1)
                    assert ch.n == D_LINKS


_INS = ["x", "norm_mix", "w_in", "conv_w", "q_norm", "w_uq", "kv_norm", "w_ukv", "q_head_norm", "k_head_norm",
        "w_o", "norm_ffn", "w_router", "b_router", "w_gate_up", "b_gate_up", "w_down", "b_down"]


def kernel(**inputs):
    import numpy as _np
    import concourse.bacc as _bacc
    from concourse.bass_utils import run_bass_kernel_spmd as _run

    nc = _bacc.Bacc("TRN2", target_bir_lowering=False, num_devices=1)
    arrays, args = {}, {}
    for name in _INS:
        a = _np.ascontiguousarray(inputs[name])
        arrays[f"in_{name}"] = a
        args[name] = nc.dram_tensor(f"in_{name}", a.shape, mybir.dt.from_np(a.dtype), kind="ExternalInput").ap()
    out = nc.dram_tensor("out_0", (1, SEQ, D), F32, kind="ExternalOutput").ap()
    build(nc, args, out)
    r = _run(nc, [arrays], core_ids=[0])
    return r.results[0]["out_0"]
```
